# Optimizing a Trainium2 kernel written in Bass

```python
import jax, jax.numpy as jnp
from jax import lax
import numpy as np

D_MODEL = 1024
BATCH = 1
SEQ = 256
DEPTH = 2

RET_HEADS = 4
RET_HEAD_DIM = D_MODEL // 8
D_RET = RET_HEADS * RET_HEAD_DIM
RET_CHUNK = 128
ROPE_BASE = 10000.0
POOL_WINDOWS = (2, 4, 8, 16)
POOL_GROUPS = 4
POOL_GROUP_DIM = D_MODEL // 8
D_POOL = POOL_GROUPS * POOL_GROUP_DIM
POOL_OUT_GROUP_DIM = D_MODEL // POOL_GROUPS
D_CONV = D_MODEL // 2
CONV_WIDTH = 31
D_FF = 2816
N_BRANCHES = 3
EPS = 1e-6
D_IN = 4 * D_RET + D_POOL + 2 * D_CONV + N_BRANCHES * D_MODEL

kernel_name = "hybrid_retention_pool_conformer_macaron"

def rmsnorm(x, g):
    xf = x.astype(jnp.float32)
    y = xf * lax.rsqrt(jnp.mean(xf * xf, axis=-1, keepdims=True) + EPS)
    return (y * g.astype(jnp.float32)).astype(x.dtype)

def layernorm(x, g, b):
    xf = x.astype(jnp.float32)
    mu = jnp.mean(xf, axis=-1, keepdims=True)
    var = jnp.mean(jnp.square(xf - mu), axis=-1, keepdims=True)
    y = (xf - mu) * lax.rsqrt(var + EPS)
    return (y * g.astype(jnp.float32) + b.astype(jnp.float32)).astype(x.dtype)

def swiglu_ffn(x, w_in, w_out):
    gate, up = jnp.split(x @ w_in, 2, axis=-1)
    return (jax.nn.silu(gate) * up) @ w_out

def rotary(x, cos, sin):
    half = x.shape[-1] // 2
    x1, x2 = x[..., :half], x[..., half:]
    return jnp.concatenate([x1 * cos - x2 * sin, x2 * cos + x1 * sin], axis=-1)

def retention(q, k, v, positions):
    in_dtype = q.dtype
    B, S, _ = q.shape
    H, dh, C = RET_HEADS, RET_HEAD_DIM, RET_CHUNK
    N = S // C
    q = q.astype(jnp.float32).reshape(B, S, H, dh)
    k = k.astype(jnp.float32).reshape(B, S, H, dh)
    v = v.astype(jnp.float32).reshape(B, S, H, dh)
    inv_freq = ROPE_BASE ** (-jnp.arange(dh // 2, dtype=jnp.float32) / (dh // 2))
    ang = positions.astype(jnp.float32)[..., None] * inv_freq
    cos = jnp.cos(ang)[:, :, None, :]
    sin = jnp.sin(ang)[:, :, None, :]
    q = rotary(q, cos, sin)
    k = rotary(k, cos, sin) * (dh ** -0.5)
    qc = q.reshape(B, N, C, H, dh)
    kc = k.reshape(B, N, C, H, dh)
    vc = v.reshape(B, N, C, H, dh)
    log_gamma = jnp.log1p(-(2.0 ** (-5.0 - jnp.arange(H, dtype=jnp.float32))))
    idx = jnp.arange(C, dtype=jnp.float32)
    diff = idx[:, None] - idx[None, :]
    decay_in = jnp.where(diff >= 0, jnp.exp(log_gamma[:, None, None] * jnp.maximum(diff, 0.0)), 0.0)
    scores = jnp.einsum('bnihd,bnjhd->bnhij', qc, kc) * decay_in
    inner = jnp.einsum('bnhij,bnjhe->bnihe', scores, vc)
    kv_decay = jnp.exp(log_gamma[:, None] * (C - 1 - idx))
    chunk_kv = jnp.einsum('bnjhd,hj,bnjhe->nbhde', kc, kv_decay, vc)
    chunk_decay = jnp.exp(log_gamma * C)[None, :, None, None]

    def step(state, kv):
        return state * chunk_decay + kv, state

    _, prev_states = lax.scan(step, jnp.zeros_like(chunk_kv[0]), chunk_kv)
    q_decay = jnp.exp(log_gamma[:, None] * (idx + 1.0))
    cross = jnp.einsum('bnihd,hi,nbhde->bnihe', qc, q_decay, prev_states)
    out = (inner + cross).reshape(B, S, H, dh)
    out = out * lax.rsqrt(jnp.mean(out * out, axis=-1, keepdims=True) + EPS)
    return out.reshape(B, S, D_RET).astype(in_dtype)

def pool_mixer(p, w_pool, pool_scale):
    B, S, _ = p.shape
    G = POOL_GROUP_DIM
    pf = p.astype(jnp.float32)
    csum = jnp.pad(jnp.cumsum(pf, axis=1), ((0, 0), (1, 0), (0, 0)))
    t = jnp.arange(S, dtype=jnp.float32)
    outs = []
    for gi, w in enumerate(POOL_WINDOWS):
        c = csum[:, :, gi * G:(gi + 1) * G]
        upper = c[:, 1:]
        lower = jnp.concatenate([jnp.zeros((B, w - 1, G), jnp.float32), c[:, :S - w + 1]], axis=1)
        count = jnp.minimum(t + 1.0, float(w))[None, :, None]
        pooled = (upper - lower) / count - pf[:, :, gi * G:(gi + 1) * G]
        outs.append(jnp.einsum('bsg,go->bso', pooled.astype(p.dtype), w_pool[gi]))
    return jnp.concatenate(outs, axis=-1) * pool_scale

def conv_module(c_in, conv_w, conv_b, ln_g, ln_b, w_conv_out):
    a, b = jnp.split(c_in, 2, axis=-1)
    u = a * jax.nn.sigmoid(b)
    u_pad = jnp.pad(u, ((0, 0), (CONV_WIDTH - 1, 0), (0, 0)))
    y = lax.conv_general_dilated(u_pad, conv_w[:, None, :], window_strides=(1,), padding='VALID',
                                 dimension_numbers=('NWC', 'WIO', 'NWC'),
                                 feature_group_count=D_CONV) + conv_b
    y = jax.nn.silu(layernorm(y, ln_g, ln_b))
    return y @ w_conv_out

def setup_inputs(seed: int = 0) -> dict:
    key = jax.random.key(seed)
    ks = jax.random.split(key, 24)
    f32 = jnp.float32
    L, D = DEPTH, D_MODEL

    def nrm(k, shape, scale):
        return jax.random.normal(k, shape, f32) * scale

    def gain(k, shape):
        return 1.0 + 0.05 * jax.random.normal(k, shape, f32)

    return {
        "x": jax.random.normal(ks[0], (BATCH, SEQ, D), f32),
        "positions": jnp.broadcast_to(jnp.arange(SEQ, dtype=jnp.int32)[None, :], (BATCH, SEQ)),
        "norm_ffn1": gain(ks[1], (L, D)),
        "w_ffn1_in": nrm(ks[2], (L, D, 2 * D_FF), D ** -0.5),
        "w_ffn1_out": nrm(ks[3], (L, D_FF, D), D_FF ** -0.5),
        "norm_mix": gain(ks[4], (L, D)),
        "w_in": nrm(ks[5], (L, D, D_IN), D ** -0.5),
        "gate_bias": nrm(ks[6], (L, N_BRANCHES * D), 0.02),
        "w_ret_out": nrm(ks[7], (L, D_RET, D), D_RET ** -0.5),
        "w_pool": nrm(ks[8], (L, POOL_GROUPS, POOL_GROUP_DIM, POOL_OUT_GROUP_DIM), POOL_GROUP_DIM ** -0.5),
        "pool_scale": gain(ks[9], (L, D)),
        "conv_w": nrm(ks[10], (L, CONV_WIDTH, D_CONV), CONV_WIDTH ** -0.5),
        "conv_b": nrm(ks[11], (L, D_CONV), 0.02),
        "conv_ln_g": gain(ks[12], (L, D_CONV)),
        "conv_ln_b": nrm(ks[13], (L, D_CONV), 0.02),
        "w_conv_out": nrm(ks[14], (L, D_CONV, D), D_CONV ** -0.5),
        "w_out": nrm(ks[15], (L, D, D), D ** -0.5),
        "norm_ffn2": gain(ks[16], (L, D)),
        "w_ffn2_in": nrm(ks[17], (L, D, 2 * D_FF), D ** -0.5),
        "w_ffn2_out": nrm(ks[18], (L, D_FF, D), D_FF ** -0.5),
        "norm_final": gain(ks[19], (D,)),
    }

def reference(x, positions, norm_ffn1, w_ffn1_in, w_ffn1_out, norm_mix, w_in, gate_bias,
              w_ret_out, w_pool, pool_scale, conv_w, conv_b, conv_ln_g, conv_ln_b, w_conv_out,
              w_out, norm_ffn2, w_ffn2_in, w_ffn2_out, norm_final):
    B, S, D = x.shape
    split_points = np.cumsum([D_RET, D_RET, D_RET, D_RET, D_POOL, 2 * D_CONV]).tolist()
    for l in range(DEPTH):
        x = x + 0.5 * swiglu_ffn(rmsnorm(x, norm_ffn1[l]), w_ffn1_in[l], w_ffn1_out[l])
        u = rmsnorm(x, norm_mix[l])
        proj = u @ w_in[l]
        q, k, v, g, p, c, gates = jnp.split(proj, split_points, axis=-1)
        y_ret = (retention(q, k, v, positions) * jax.nn.silu(g)) @ w_ret_out[l]
        y_pool = pool_mixer(p, w_pool[l], pool_scale[l])
        y_conv = conv_module(c, conv_w[l], conv_b[l], conv_ln_g[l], conv_ln_b[l], w_conv_out[l])
        gates = jax.nn.sigmoid(gates + gate_bias[l]).reshape(B, S, N_BRANCHES, D)
        merged = gates[:, :, 0] * y_ret + gates[:, :, 1] * y_pool + gates[:, :, 2] * y_conv
        x = x + merged @ w_out[l]
        x = x + 0.5 * swiglu_ffn(rmsnorm(x, norm_ffn2[l]), w_ffn2_in[l], w_ffn2_out[l])
    return rmsnorm(x, norm_final)


_drawn_inputs = setup_inputs


def setup_inputs(seed=0):
    import zlib

    import numpy as np

    out = dict(_drawn_inputs(seed))
    spreads = {}
    factors = {'gate_bias': 8.0, 'conv_b': 3.251, 'conv_ln_b': 7.02}
    for name, (base, spread) in spreads.items():
        noise = np.random.default_rng([zlib.crc32(name.encode()), seed]).standard_normal(out[name].shape)
        drawn = base * np.exp(spread * noise) if base else spread * noise
        out[name] = __import__('jax').numpy.asarray(drawn.astype(out[name].dtype))
    for name, factor in factors.items():
        out[name] = (out[name] * factor).astype(out[name].dtype)
    return out
```

```python
from contextlib import ExitStack

import concourse.bass as bass
import numpy as np
from concourse import mybir

ALU = mybir.AluOpType
ACT = mybir.ActivationFunctionType
F32 = mybir.dt.float32
F32R = mybir.dt.float32r
BF16 = mybir.dt.bfloat16
I32 = mybir.dt.int32
U8 = mybir.dt.uint8

P = 128
L = 2
D = 1024
S = 256
T = S // P
KT = D // P
F = 2816
FT = F // P
FB = F // 256
HEADS, DH = 4, 128
GROUPS = 4
CH = 4
TAPS = 31
PAD = TAPS - 1
NB = 512
EPS = 1e-6
ROPE_BASE = 10000.0
WINDOWS = (2, 4, 8, 16)

OUT_CHUNKS = [list(range(4)), [4, 5]] + [list(range(k, k + 4)) for k in range(6, FT, 4)]
FFN_CHUNKS = FB + len(OUT_CHUNKS)
MIX = FFN_CHUNKS
(M_A, M_B, M_Q, M_K, M_V, M_G, M_P, M_GATE_POOL, _, M_POOL, M_GATE_RET, _, M_RET, M_GATE_CONV, _,
 M_CONV, M_OUT, _) = range(MIX, MIX + 18)
FFN2 = MIX + 18
CHUNKS = FFN2 + FFN_CHUNKS
assert CHUNKS % 2 == 0
HALVES = 2 * CHUNKS
HALF_AT = 2048
HALF = P * HALF_AT
W_IN_BLOCK = {M_A: 5, M_B: 6, M_Q: 0, M_K: 1, M_V: 2, M_G: 3, M_P: 4, M_GATE_POOL: 9,
              M_GATE_POOL + 1: 10, M_GATE_RET: 7, M_GATE_RET + 1: 8, M_GATE_CONV: 11,
              M_GATE_CONV + 1: 12}
POOLED, RET, CONV = 0, 1, 2
GATE_OF = {POOLED: 1, RET: 0, CONV: 2}
M_GATE = [M_GATE_POOL, M_GATE_RET, M_GATE_CONV]
M_BRANCH = [M_POOL, M_RET, M_CONV]

ACC_USE = {}
_n = [0, 0]


def _plan_accumulators():
    def use(g, b):
        ACC_USE[g, b] = _n[b]
        _n[b] += 1

    for g in range(FB):
        use(g, g % 2)
    for b in (0, 1):
        use(FB, b)
    for g in range(MIX, M_POOL):
        use(g, (g - MIX) % 2)
    for br in range(3):
        if br:
            use(M_GATE[br], 0)
            use(M_GATE[br] + 1, 1)
        for b in (0, 1):
            use(M_BRANCH[br], b)
    for b in (0, 1):
        use(M_OUT, b)
    for b in range(FB):
        use(FFN2 + b, b % 2)
    for b in (0, 1):
        use(FFN2 + FB, b)


_plan_accumulators()
ACC_USES = tuple(_n)


def in_bank(g):
    return 0 if (g, 0) in ACC_USE else 1


def out_bank(g, n):
    return n if g in (M_RET, M_CONV, M_OUT) else 1 - n


TR = {}


def _plan_transposes():
    order = []
    for norm in (0, 1, 3):
        quarter = [("x", norm, t, c) for t in range(T) for c in (0, 1)]
        if norm == 1:
            order += quarter + [("u", t) for t in range(T)]
            order += [(w, t) for w in "qk" for t in range(T)]
            order += [("pooled", i) for i in (0, 1)] + [("scores", h) for h in range(HEADS)]
            order += [("ret", t) for t in range(T)] + [("y", t) for t in range(T)]
            order += [("yn", i) for i in (0, 1)]
            order += [("x", 2, t, c) for t in range(T) for c in (0, 1)]
        else:
            order += quarter + [("h", norm // 3, b) for b in range(FB)]
    TR.update({name: i for i, name in enumerate(order)})


_plan_transposes()
TR_USES = len(TR)
assert TR_USES % 2 == 0

PAR_GAIN = {0: 0, 1: KT, 3: 2 * KT}
PAR_CONV_W = 3 * KT
PAR_CONV_B = PAR_CONV_W + CH * TAPS
PAR_LN_G = PAR_CONV_B + CH
PAR_LN_B = PAR_LN_G + CH
PARAMS = PAR_LN_B + CH

TWO_PI_PARTS = []
_rest = 2 * np.pi
for _ in range(3):
    _e = 2.0 ** (np.floor(np.log2(_rest)) - 7)
    TWO_PI_PARTS.append(float(np.floor(_rest / _e) * _e))
    _rest -= TWO_PI_PARTS[-1]
TWO_PI_PARTS.append(float(np.float32(_rest)))
ANGLES_READY = 5 + T + 2 + len(TWO_PI_PARTS) + 1
ROUND = 1.5 * 2.0 ** 23
PI_BELOW = 3.1415925


def trunk(nc, x_in, positions, weights_in, gate_bias, pool_scale, norm_final, params, ident_in,
          inv_freq_in, decay_in, band_in, out):
    with ExitStack() as ctx:
        def sb(name, shape, dt=F32):
            return ctx.enter_context(nc.sbuf_tensor(name, shape, dt))

        def sem(name):
            return ctx.enter_context(nc.semaphore(name))

        raw = sb("raw", [P, 2, 4096])
        w_hi = sb("w_hi", [P, 2, 4096], F32R)
        w_lo = sb("w_lo", [P, 2, 4096], F32R)
        x = sb("x", [P, T, D])
        xg = sb("xg", [P, 2, 4, P])
        xT_hi = sb("xT_hi", [P, KT, S], F32R)
        xT_lo = sb("xT_lo", [P, KT, S], F32R)
        sideT_hi = sb("sideT_hi", [P, 4, S], F32R)
        sideT_lo = sb("sideT_lo", [P, 4, S], F32R)
        squares = sb("squares", [P, D], BF16)
        ident = sb("ident", [P, P])
        decay = sb("decay", [P, HEADS, S])
        band = sb("band", [P, GROUPS, S + P])
        all_params = sb("all_params", [P, L, PARAMS])
        par = sb("par", [P, PARAMS])
        cos = sb("cos", [P, T, DH // 2])
        sin = sb("sin", [P, T, 2, DH // 2])
        small = sb("small", [P, 8])
        meansq = sb("meansq", [P, T])
        meansq_eps = sb("meansq_eps", [P, T])
        rs = sb("rs", [P, T])
        half_rs = sb("half_rs", [P, T])
        head_sumsq = sb("head_sumsq", [P, T, HEADS])
        head_meansq = sb("head_meansq", [P, T, HEADS])
        head_meansq_eps = sb("head_meansq_eps", [P, T, HEADS])
        head_rs = sb("head_rs", [P, T, HEADS])
        ln_stats = sb("ln_stats", [P, T, 6])
        ln_mean_var = sb("ln_mean_var", [P, T, 2])
        ln_var = sb("ln_var", [P, T])
        ln_rstd = sb("ln_rstd", [P, T])

        arena_from = nc.sbuf_base
        arena_at = -(-arena_from // 32) * 32
        end = [arena_at]

        def place(name, shape, dt=F32):
            t = nc.alloc_sbuf_tensor_at(name, shape, dt, offset=end[0])
            end[0] += 4 * int(np.prod(shape[1:]))
            return t

        inv_freq = place("inv_freq", [P, DH // 2])
        pos = place("pos", [P, 8], I32)
        posf = place("posf", [P, 8])
        end[0] = arena_at
        hT_hi = place("hT_hi", [P, FT, S], F32R)
        hT_lo = place("hT_lo", [P, FT, S], F32R)
        silu_gate = place("silu_gate", [P, T, 256])
        h = place("h", [P, T, 256])
        ffn_end, end[0] = end[0], arena_at
        ua = place("ua", [P, T, NB])
        ub = place("ub", [P, T, NB])
        qk = place("qk", [P, 2, T, NB])
        v = place("v", [P, T, NB])
        g_silu = place("g_silu", [P, T, NB])
        pin = place("pin", [P, T, NB])
        uT = place("uT", [P, CH, 288])
        y = place("y", [P, CH, S])
        qkT = place("qkT", [P, 2, HEADS, S])
        st = place("st", [P, 2, S + P])
        gates = place("gates", [P, T, D])
        end[0] = max(end[0], ffn_end)
        bias = place("bias", [P, D])
        arena = sb("arena", [P, end[0] - arena_from], U8)
        merged = qk
        rot = st
        ysilu = v

        acc = ctx.enter_context(nc.psum_tensor("acc", [P, T, 2, NB], F32))
        tr = ctx.enter_context(nc.psum_tensor("tr", [P, 2, NB], F32))
        ret = ctx.enter_context(nc.psum_tensor("ret", [P, T, NB], F32))

        x_landed = sem("x_landed")
        consts_landed = sem("consts_landed")
        raw_landed = [[sem(f"raw_landed{s}{h}") for h in (0, 1)] for s in (0, 1)]
        tables_landed = sem("tables_landed")
        bias_landed = sem("bias_landed")
        scale_landed = sem("scale_landed")
        stored = sem("stored")
        hi_split = sem("hi_split")
        lo_split = sem("lo_split")
        lo_split_pool = sem("lo_split_pool")
        mm_done = sem("mm_done")
        taken = [[sem(f"acc_taken{t}{b}") for b in (0, 1)] for t in range(T)]
        tr_full = sem("tr_full")
        tr_taken = [sem(f"tr_taken{b}") for b in (0, 1)]
        xT_hi_ready = sem("xT_hi_ready")
        xT_lo_ready = sem("xT_lo_ready")
        hT_hi_ready = sem("hT_hi_ready")
        silu_ready = sem("silu_ready")
        meansq_ready = sem("meansq_ready")
        eps_added = sem("eps_added")
        rs_ready = sem("rs_ready")
        pow_done = sem("pow_done")
        par_ready = sem("par_ready")
        u_ready = sem("u_ready")
        pad_zero = sem("pad_zero")
        conv_step = sem("conv_step")
        rotary_step = sem("rotary_step")
        inner_done = sem("inner_done")
        head_sumsq_ready = sem("head_sumsq_ready")
        head_meansq_ready = sem("head_meansq_ready")
        head_eps_added = sem("head_eps_added")
        head_rs_ready = sem("head_rs_ready")
        ret_ready = sem("ret_ready")
        side_hi_ready = sem("side_hi_ready")
        conv_lo_ready = sem("conv_lo_ready")
        gate_ready = sem("gate_ready")
        gate_scaled = sem("gate_scaled")
        merged_ret = sem("merged_ret")
        merged_all = sem("merged_all")
        ln_stats_ready = sem("ln_stats_ready")
        ln_mean_ready = sem("ln_mean_ready")
        ln_var_ready = sem("ln_var_ready")
        ln_rstd_ready = sem("ln_rstd_ready")
        setup_dve = sem("setup_dve")
        setup_act = sem("setup_act")
        setup_pool = sem("setup_pool")
        out_ready = sem("out_ready")

        def wait_slot_free(e, l, g):
            e.wait_ge(mm_done, l * HALVES + (2 * g + 2))

        def wait_product(e, l, g, t):
            e.wait_ge(mm_done, l * HALVES + (2 * g + t + 5))

        def wait_hi(e, l, g, half):
            e.wait_ge(hi_split, l * HALVES + (2 * g + half + 1))

        def wait_split(e, l, g, half):
            e.wait_ge(lo_split, l * HALVES + (2 * g + half + 5))
            e.wait_ge(lo_split_pool, l * HALVES + (2 * g + half + 5))

        def wait_acc_free(e, l, g, t, b, j=0):
            e.wait_ge(taken[t][b], l * ACC_USES[b] + (j + (ACC_USE[g, b] + 1)))

        def wait_acc_taken(e, l, g, t, b, j=0):
            e.wait_ge(taken[t][b], l * ACC_USES[b] + (j + (ACC_USE[g, b] + 2)))

        def wait_tr_free(e, l, name, j=0):
            k = TR[name]
            e.wait_ge(tr_taken[k % 2], l * (TR_USES // 2) + (j + (k // 2 + 1)))

        def wait_tr_taken(e, l, name, j=0):
            k = TR[name]
            e.wait_ge(tr_taken[k % 2], l * (TR_USES // 2) + (j + (k // 2 + 2)))

        def wait_tr_full(e, l, name, j=0):
            e.wait_ge(tr_full, l * TR_USES + (j * 2 + (TR[name] + 1)))

        def bank(name):
            return tr[:, TR[name] % 2, :]

        def tokens(t):
            return slice(t * P, (t + 1) * P)

        def columns(n):
            return slice(n * NB, (n + 1) * NB)

        NORM_AT = {0: 0, 1: 1, 3: 2}
        XT_LO_AT = {0: 0, 1: 4, 3: 8}
        def vector_share(g):
            n = half_size[g]
            return n // 8 if g == 0 else n // 2 if M_G <= g <= M_OUT else 3 * n // 4

        half_size = {}
        for g in range(CHUNKS):
            half_size[g] = 2048
        half_size[FB + 1] = half_size[FFN2 + FB + 1] = 1024
        half_size[M_POOL] = 512

        block = ctx.enter_context(nc.Block())

        @block.sync
        def _(sp):
            sp.dma_start(pos[:, 0:T], positions).then_inc(consts_landed, 16)
            sp.dma_start(inv_freq[:], inv_freq_in).then_inc(consts_landed, 16)
            sp.dma_start(x[:], x_in.rearrange("a (t p) d -> p (a t) d", p=P)).then_inc(x_landed, 16)
            sp.wait_ge(consts_landed, 16 * 4)

            def load(l, g, j=0):
                n = half_size[g]
                for half in (0, 1):
                    at = sp.snap(l * (HALVES * HALF) + (j * (4 * HALF) + (2 * g + half) * HALF))
                    sp.wait_ge(lo_split, l * HALVES + (j * 4 + (2 * g + half + 1)))
                    sp.wait_ge(lo_split_pool, l * HALVES + (j * 4 + (2 * g + half + 1)))
                    sp.dma_start(raw[:, g % 2, half * HALF_AT:half * HALF_AT + n],
                                 weights_in[bass.ds(at, HALF)].rearrange(
                                     "(p n) -> p n", p=P)[:, 0:n]
                                 ).then_inc(raw_landed[g % 2][half], 16)

            with nc.sync.Fori(0, L) as l:
                for g0 in (0, FFN2):
                    load(l, g0)
                    with nc.sync.Fori(0, FB // 2) as j:
                        load(l, g0 + 1, j)
                        load(l, g0 + 2, j)
                    for g in range(g0 + FB, FFN2 if g0 == 0 else CHUNKS):
                        load(l, g)
            for t in range(T):
                sp.wait_ge(out_ready, t + 1)
                sp.dma_start(out.rearrange("a (t p) d -> p (a t) d", p=P)[:, t, :], x[:, t, :]
                             ).then_inc(stored, 16)
            sp.wait_ge(stored, 16 * T)

        @block.tensor
        def _(pe):
            pe.sem_inc(mm_done, 4)
            pe.wait_ge(consts_landed, 16 * 4)

            def product(o, lhs, rhs, first, last):
                (a_hi, a_lo), (b_hi, b_lo) = lhs, rhs
                nc.tensor.matmul(o, a_hi, b_hi, start=first, stop=False)
                nc.tensor.matmul(o, a_hi, b_lo, start=False, stop=False)
                return nc.tensor.matmul(o, a_lo, b_hi, start=False, stop=last)

            def weights(g, a, n):
                s = slice(a, a + n)
                return w_hi[:, g % 2, s], w_lo[:, g % 2, s]

            def xT(k, t):
                return xT_hi[:, k, tokens(t)], xT_lo[:, k, tokens(t)]

            def in_block(l, g, t, j=0, norm=None, mid=None):
                b = in_bank(g)
                wait_acc_free(pe, l, g, t, b, j)
                for half in (0, 1):
                    if t == 0:
                        jl = l * HALVES + (j * 4 + (2 * g + half + 5))
                        pe.wait_ge(lo_split, jl)
                        pe.wait_ge(lo_split_pool, jl)
                    if norm is not None:
                        pe.wait_ge(xT_lo_ready, l * 12 + (XT_LO_AT[norm] + 2 * t + half + 1))
                    for k in range(4 * half, 4 * half + 4):
                        mm = product(acc[:, t, b, :], xT(k, t), weights(g, k * NB, NB),
                                     k == 0, k == KT - 1)
                    if mid is not None and half == 0:
                        mid()
                mm.then_inc(mm_done, 1)

            def wide(l, g, t, lhs, ks, first, last, use, mid=None):
                m = len(ks) // 2
                for n in (0, 1):
                    b = out_bank(use, n)
                    if first:
                        wait_acc_free(pe, l, use, t, b)
                    for i, k in enumerate(ks):
                        if t == 0 and n == 0 and i % m == 0:
                            wait_split(pe, l, g, i // m)
                        mm = product(acc[:, t, b, :], lhs(k, t),
                                     weights(g, i // m * HALF_AT + i % m * D + n * NB, NB),
                                     first and i == 0, last and i == len(ks) - 1)
                    if mid is not None and n == 0:
                        mid()
                mm.then_inc(mm_done, 1)

            def wide_part(l, g, t, lhs, ks, first, use):
                m = len(ks) // 2
                if first:
                    for b in (out_bank(use, 0), out_bank(use, 1)):
                        wait_acc_free(pe, l, use, t, b)
                for i, k in enumerate(ks):
                    if t == 0 and i % m == 0:
                        wait_split(pe, l, g, i // m)
                    a_hi, a_lo = lhs(k, t)
                    at = i // m * HALF_AT + i % m * D
                    parts = [weights(g, at + n * NB, NB) for n in (0, 1)]
                    accs = [acc[:, t, out_bank(use, n), :] for n in (0, 1)]
                    for n in (0, 1):
                        nc.tensor.matmul(accs[n], a_hi, parts[n][0], start=first and i == 0,
                                         stop=False)
                        nc.tensor.matmul(accs[n], a_hi, parts[n][1], start=False, stop=False)
                    for n in (0, 1):
                        mm = nc.tensor.matmul(accs[n], a_lo, parts[n][0], start=False, stop=False)
                mm.then_inc(mm_done, 1)

            def transpose4(l, name, sources, j=0):
                wait_tr_free(pe, l, name, j)
                for i, s in enumerate(sources):
                    mm = nc.tensor.transpose(bank(name)[:, i * P:(i + 1) * P], s, ident[:])
                mm.then_inc(tr_full, 1)

            def turn_x(l, norm, t):
                for c in (0, 1):
                    if norm == 0:
                        b = out_bank(FFN2 + FB, c)
                        pe.wait_ge(taken[t][b], l * ACC_USES[b] + 1)
                    else:
                        g = FB if norm == 1 else M_OUT
                        wait_acc_taken(pe, l, g, t, out_bank(g, c))
                    transpose4(l, ("x", norm, t, c),
                               [x[:, t, (4 * c + i) * P:(4 * c + i + 1) * P] for i in range(4)])

            def turn_merged(l, t):
                for c in (0, 1):
                    pe.wait_ge(merged_all, l * 4 + (2 * t + c + 1))
                    transpose4(l, ("x", 2, t, c),
                               [merged[:, t, c, i * P:(i + 1) * P] for i in range(4)])

            def turn_h(l, f, b, j=0):
                g = f * FFN2 + b
                for t in range(T):
                    wait_acc_taken(pe, l, g, t, in_bank(g), j)
                transpose4(l, ("h", f, b),
                           [h[:, t, c * P:(c + 1) * P] for c in (0, 1) for t in range(T)], j)

            def ffn(l, f, next_turn):
                g0, norm = f * FFN2, 3 * f
                in_block(l, g0, 0, norm=norm, mid=lambda: turn_x(l, norm, 1))
                in_block(l, g0, 1, norm=norm)
                with nc.tensor.Fori(0, FB // 2) as j:
                    for b in (1, 2):
                        in_block(l, g0 + b, 0, j)
                        turn_h(l, f, b - 1, j)
                        in_block(l, g0 + b, 1, j)

                def hT(k, t):
                    return hT_hi[:, k, tokens(t)], hT_lo[:, k, tokens(t)]

                last = len(OUT_CHUNKS) - 1
                for i, ks in enumerate(OUT_CHUNKS):
                    g = g0 + FB + i
                    wait_tr_taken(pe, l, ("h", f, ks[-1] // 2 - 1))
                    wait_tr_taken(pe, l, ("h", f, ks[-1] // 2))
                    if i < last:
                        wide_part(l, g, 0, hT, ks, i == 0, g0 + FB)
                        if i == 0:
                            turn_h(l, f, FB - 1)
                        wide_part(l, g, 1, hT, ks, i == 0, g0 + FB)
                    else:
                        wide(l, g, 0, hT, ks, False, True, g0 + FB)
                        wide(l, g, 1, hT, ks, False, True, g0 + FB, mid=next_turn)

            def side(k, t):
                return sideT_hi[:, k, tokens(t)], sideT_lo[:, k, tokens(t)]

            def pooled(l, i):
                name = ("pooled", i)
                pe.wait_ge(tables_landed, 32)
                wait_tr_free(pe, l, name)
                for c in (0, 1):
                    grp = 2 * i + c
                    s = slice(grp * P, (grp + 1) * P)
                    o = bank(name)[:, c * S:(c + 1) * S]
                    nc.tensor.matmul(o, pin[:, 0, s], band[:, grp, 0:S], start=True, stop=False)
                    mm = nc.tensor.matmul(o[:, P:S], pin[:, 1, s], band[:, grp, S:S + P],
                                          start=False, stop=True)
                mm.then_inc(tr_full, 1)

            def scores(l, hd):
                name = ("scores", hd)
                wait_tr_free(pe, l, name)
                nc.tensor.matmul(bank(name)[:, 0:S], qkT[:, 1, hd, 0:P], qkT[:, 0, hd, :],
                                 start=True, stop=True)
                nc.tensor.matmul(bank(name)[:, S:S + P], qkT[:, 1, hd, P:S], qkT[:, 0, hd, P:S],
                                 start=True, stop=True).then_inc(tr_full, 1)

            def inner(l, hd):
                wait_tr_taken(pe, l, ("scores", hd))
                s = slice(hd * P, (hd + 1) * P)
                nc.tensor.matmul(ret[:, 0, s], st[:, hd % 2, 0:P], v[:, 0, s],
                                 start=True, stop=True)
                nc.tensor.matmul(ret[:, 1, s], st[:, hd % 2, P:S], v[:, 0, s],
                                 start=True, stop=False)
                nc.tensor.matmul(ret[:, 1, s], st[:, hd % 2, S:S + P], v[:, 1, s],
                                 start=False, stop=True).then_inc(inner_done, 1)

            def mixer(l):
                in_block(l, M_A, 0, norm=1, mid=lambda: turn_x(l, 1, 1))
                in_block(l, M_A, 1, norm=1)
                in_block(l, M_B, 0)
                in_block(l, M_B, 1)
                in_block(l, M_Q, 0)
                for t in range(T):
                    pe.wait_ge(u_ready, l * T + (t + 1))
                    transpose4(l, ("u", t), [ua[:, t, c * P:(c + 1) * P] for c in range(CH)])
                in_block(l, M_Q, 1)
                for g in (M_K, M_V, M_G):
                    in_block(l, g, 0)
                    in_block(l, g, 1)
                in_block(l, M_P, 0)
                for i, w in enumerate("qk"):
                    for t in range(T):
                        pe.wait_ge(rotary_step, l * 16 + (8 * i + 4 * t + 4))
                        transpose4(l, (w, t), [qk[:, i, t, c * P:(c + 1) * P]
                                               for c in range(HEADS)])
                in_block(l, M_P, 1)
                in_block(l, M_GATE_POOL, 0)
                for t in range(T):
                    wait_acc_taken(pe, l, M_P, t, in_bank(M_P))
                pooled(l, 0)
                pooled(l, 1)
                in_block(l, M_GATE_POOL, 1)
                in_block(l, M_GATE_POOL + 1, 0)
                wait_tr_taken(pe, l, ("k", 0))
                wait_tr_taken(pe, l, ("k", 1))
                scores(l, 0)
                scores(l, 1)
                in_block(l, M_GATE_POOL + 1, 1)
                inner(l, 0)
                scores(l, 2)
                inner(l, 1)
                scores(l, 3)
                for t in range(T):
                    for n in (0, 1):
                        b = out_bank(M_POOL, n)
                        wait_acc_free(pe, l, M_POOL, t, b)
                        if t == 0:
                            wait_split(pe, l, M_POOL, n)
                        for grp in (2 * n, 2 * n + 1):
                            c = (grp - 2 * n) * 256
                            mm = product(acc[:, t, b, c:c + 256], side(grp, t),
                                         weights(M_POOL, n * HALF_AT + c, 256), True, True)
                    mm.then_inc(mm_done, 1)
                in_block(l, M_GATE_RET, 0)
                inner(l, 2)
                inner(l, 3)
                in_block(l, M_GATE_RET, 1)
                in_block(l, M_GATE_RET + 1, 0)
                for t in range(T):
                    pe.wait_ge(ret_ready, l * T + (t + 1))
                    transpose4(l, ("ret", t), [ua[:, t, c * P:(c + 1) * P] for c in range(HEADS)])
                in_block(l, M_GATE_RET + 1, 1)
                for t in range(T):
                    wait_tr_taken(pe, l, ("ret", t))
                for t in range(T):
                    wide(l, M_RET, t, side, range(4), True, True, M_RET)
                in_block(l, M_GATE_CONV, 0)
                for t in range(T):
                    pe.wait_ge(conv_step, l * (CH * TAPS) + CH * TAPS)
                    transpose4(l, ("y", t), [y[:, c, tokens(t)] for c in range(CH)])
                in_block(l, M_GATE_CONV, 1)
                in_block(l, M_GATE_CONV + 1, 0)
                wait_tr_taken(pe, l, ("y", 0))
                wait_tr_taken(pe, l, ("y", 1))
                for i in (0, 1):
                    transpose4(l, ("yn", i),
                               [pin[:, t, (2 * i + c) * P:(2 * i + c + 1) * P]
                                for c in (0, 1) for t in range(T)])
                in_block(l, M_GATE_CONV + 1, 1)
                pe.wait_ge(conv_lo_ready, l * 2 + 2)
                wide(l, M_CONV, 0, side, range(4), True, True, M_CONV)
                wide(l, M_CONV, 1, side, range(4), True, True, M_CONV,
                     mid=lambda: turn_merged(l, 0))
                for i in (0, 1):
                    ks = range(4 * i, 4 * i + 4)
                    wait_tr_taken(pe, l, ("x", 2, 0, i))
                    wide(l, M_OUT + i, 0, xT, ks, i == 0, i == 1, M_OUT,
                         mid=(lambda: turn_merged(l, 1)) if i == 0 else None)
                    wait_tr_taken(pe, l, ("x", 2, 1, i))
                    wide(l, M_OUT + i, 1, xT, ks, i == 0, i == 1, M_OUT,
                         mid=(lambda: turn_x(l, 3, 0)) if i == 1 else None)

            with nc.tensor.Fori(0, L) as l:
                turn_x(l, 0, 0)
                ffn(l, 0, lambda: turn_x(l, 1, 0))
                mixer(l)
                ffn(l, 1, None)

        @block.scalar
        def _(act):
            act.dma_start(ident[:], ident_in).then_inc(consts_landed, 16)
            act.dma_start(all_params[:], params.rearrange("l p n -> p l n")
                          ).then_inc(consts_landed, 16)
            nc.scalar.preload_act_table_set("silu_and_others")
            act.wait_ge(setup_dve, ANGLES_READY)
            nc.scalar.activation(sin[:, :, 0, :], cos[:], ACT.Sin).then_inc(setup_act, 1)
            nc.scalar.activation(sin[:, :, 1, :], cos[:], ACT.Sin, scale=0.5
                                 ).then_inc(setup_act, 1)
            act.dma_start(decay[:], decay_in).then_inc(tables_landed, 16)
            act.dma_start(band[:], band_in).then_inc(tables_landed, 16)

            def split(l, g, j=0):
                n = half_size[g]
                act.wait_ge(mm_done, l * HALVES + (j * 4 + (2 * g + 2)))
                for half in (0, 1):
                    s = slice(half * HALF_AT, half * HALF_AT + n)
                    act.wait_ge(raw_landed[g % 2][half],
                                l * (16 * CHUNKS // 2) + (j * 16 + 16 * (g // 2 + 1)))
                    nc.scalar.copy(w_hi[:, g % 2, s], raw[:, g % 2, s]).then_inc(hi_split, 1)

            def xT_high(l, norm, t):
                for c in (0, 1):
                    wait_tr_taken(act, l, ("x", norm, t, c))
                    nc.scalar.copy(xT_hi[:, 4 * c:4 * c + 4, tokens(t)],
                                   xg[:, c, :, :]).then_inc(xT_hi_ready, 1)

            def merged_high(l, t):
                for c in (0, 1):
                    wait_tr_full(act, l, ("x", 2, t, c))
                    nc.scalar.activation(xT_hi[:, 4 * c:4 * c + 4, tokens(t)],
                                         bank(("x", 2, t, c)).rearrange("p (k n) -> p k n", k=4),
                                         ACT.Copy, scale=0.5).then_inc(xT_hi_ready, 1)

            def square(l, norm, t):
                for c in (0, 1):
                    if norm == 0:
                        b = out_bank(FFN2 + FB, c)
                        act.wait_ge(taken[t][b], l * ACC_USES[b] + 1)
                    else:
                        g = FB if norm == 1 else M_OUT
                        wait_acc_taken(act, l, g, t, out_bank(g, c))
                if t:
                    act.wait_ge(meansq_ready, l * 6 + (2 * NORM_AT[norm] + t))
                nc.scalar.activation(squares[:], x[:, t, :], ACT.Square,
                                     scale=D ** -0.5, accum_out=meansq[:, t:t + 1]
                                     ).then_inc(meansq_ready, 1)

            def h_high(l, f, b, j=0):
                wait_tr_full(act, l, ("h", f, b), j)
                k = 2 * b if isinstance(j, int) else j * 4 + 2 * b
                nc.scalar.copy(hT_hi[:, bass.ds(k, 2), :],
                               bank(("h", f, b)).rearrange("p (k n) -> p k n", k=2)
                               ).then_inc(hT_hi_ready, 1)

            def silu(l, f, b, j=0):
                g = f * FFN2 + b
                for t in range(T):
                    if b == 0:
                        act.wait_ge(rs_ready, l * 6 + (4 * f + t + 1))
                    act.wait_ge(mm_done, l * HALVES + (j * 4 + (2 * g + t + 5)))
                    if b:
                        wait_acc_taken(act, l, g - 1, t, in_bank(g - 1), j)
                    nc.scalar.activation(silu_gate[:, t, :], acc[:, t, in_bank(g), 0:256],
                                         ACT.Silu, scale=rs[:, t:t + 1]).then_inc(silu_ready, 1)

            def ffn(l, f):
                g0 = f * FFN2
                xT_high(l, 3 * f, 1)
                split(l, g0 + 1)
                silu(l, f, 0)
                with nc.scalar.Fori(0, FB // 2) as j:
                    nc.scalar.preload_act_table_set("silu_and_others")
                    for b in (1, 2):
                        split(l, g0 + b + 1, j)
                        h_high(l, f, b - 1, j)
                        silu(l, f, b, j)
                split(l, g0 + FB + 1)
                h_high(l, f, FB - 1)
                for i in range(2, len(OUT_CHUNKS)):
                    split(l, g0 + FB + i)

            def take(l, g, t, dst, func=ACT.Copy, scale=None):
                wait_product(act, l, g, t)
                b = in_bank(g)
                nc.scalar.activation(dst, acc[:, t, b, :], func,
                                     scale=rs[:, t:t + 1] if scale is None else scale
                                     ).then_inc(taken[t][b], 1)

            def gate_tanh(l, br, n, tiles=range(T)):
                g = M_GATE[br] + n
                for t in tiles:
                    wait_acc_taken(act, l, g, t, in_bank(g))
                    z = gates[:, t, columns(n)]
                    nc.scalar.activation(z, z, ACT.Tanh, scale=0.5).then_inc(gate_ready, 1)

            def load_bias(l, br):
                row = GATE_OF[br] * D
                act.dma_start(bias[:],
                              gate_bias.rearrange("l (o n) -> l o n", o=1)[l, :, row:row + D]
                              .broadcast_to([P, D])).then_inc(bias_landed, 16)

            def side_high(l, name, s, k):
                wait_tr_full(act, l, name)
                nc.scalar.copy(s, bank(name).rearrange("p (k n) -> p k n", k=k)
                               ).then_inc(side_hi_ready, 1)

            def mixer(l):
                xT_high(l, 1, 1)
                load_bias(l, POOLED)
                split(l, M_A + 1)
                for t in range(T):
                    act.wait_ge(rs_ready, l * 6 + (2 + t + 1))
                    take(l, M_A, t, ua[:, t, :])
                split(l, M_B + 1)
                for t in range(T):
                    take(l, M_B, t, ub[:, t, :], ACT.Tanh, half_rs[:, t:t + 1])
                split(l, M_Q + 1)
                for t in range(T):
                    name = ("u", t)
                    wait_tr_full(act, l, name)
                    act.wait_ge(pad_zero, l + 1)
                    nc.scalar.activation(uT[:, :, PAD + t * P:PAD + (t + 1) * P],
                                         bank(name).rearrange("p (c n) -> p c n", c=CH),
                                         ACT.Copy, scale=0.5).then_inc(tr_taken[TR[name] % 2], 1)
                act.dma_start(ub[:].rearrange("p t n -> p (t n)"),
                              pool_scale.rearrange("l (o n) -> l o n", o=1)[l]
                              .broadcast_to([P, D])).then_inc(scale_landed, 16)
                for t in range(T):
                    take(l, M_Q, t, qk[:, 0, t, :])
                split(l, M_K + 1)
                for t in range(T):
                    take(l, M_K, t, qk[:, 1, t, :])
                split(l, M_V + 1)
                for t in range(T):
                    take(l, M_V, t, v[:, t, :])
                split(l, M_G + 1)
                for t in range(T):
                    take(l, M_G, t, g_silu[:, t, :], ACT.Silu)
                split(l, M_P + 1)
                for i, w in enumerate("qk"):
                    for t in range(T):
                        name = (w, t)
                        wait_tr_full(act, l, name)
                        nc.scalar.copy(qkT[:, i, :, tokens(t)],
                                       bank(name).rearrange("p (h n) -> p h n", h=HEADS)
                                       ).then_inc(tr_taken[TR[name] % 2], 1)
                for t in range(T):
                    take(l, M_P, t, pin[:, t, :])
                split(l, M_GATE_POOL + 1)
                for i in (0, 1):
                    side_high(l, ("pooled", i), sideT_hi[:, 2 * i:2 * i + 2, :], 2)
                gate_tanh(l, POOLED, 0)
                split(l, M_POOL)
                gate_tanh(l, POOLED, 1, [0])
                split(l, M_GATE_RET)
                gate_tanh(l, POOLED, 1, [1])
                load_bias(l, RET)
                split(l, M_GATE_RET + 1)
                for t in range(T):
                    act.wait_ge(inner_done, l * HEADS + HEADS)
                    for hd in range(HEADS):
                        s = slice(hd * P, (hd + 1) * P)
                        nc.scalar.activation(squares[:, t * NB + hd * P:t * NB + (hd + 1) * P],
                                             ret[:, t, s], ACT.Square,
                                             accum_out=head_sumsq[:, t, hd:hd + 1]
                                             ).then_inc(head_sumsq_ready, 1)
                split(l, M_RET)
                for t in range(T):
                    side_high(l, ("ret", t), sideT_hi[:, :, tokens(t)], HEADS)
                gate_tanh(l, RET, 0)
                split(l, M_GATE_CONV)
                gate_tanh(l, RET, 1)
                load_bias(l, CONV)
                split(l, M_GATE_CONV + 1)
                gate_tanh(l, CONV, 0)
                split(l, M_CONV)
                for i in (0, 1):
                    name = ("yn", i)
                    wait_tr_full(act, l, name)
                    for c in (0, 1):
                        ch = 2 * i + c
                        a = nc.scalar.activation(
                            ysilu[:, i, c * S:(c + 1) * S], bank(name)[:, c * S:(c + 1) * S],
                            ACT.Silu, bias=par[:, PAR_LN_B + ch:PAR_LN_B + ch + 1],
                            scale=par[:, PAR_LN_G + ch:PAR_LN_G + ch + 1])
                    a.then_inc(tr_taken[TR[name] % 2], 1)
                for i in (0, 1):
                    wait_tr_taken(act, l, ("yn", i))
                    nc.scalar.copy(sideT_hi[:, 2 * i:2 * i + 2, :],
                                   ysilu[:, i, :].rearrange("p (k n) -> p k n", k=2)
                                   ).then_inc(side_hi_ready, 1)
                gate_tanh(l, CONV, 1)
                split(l, M_OUT)
                merged_high(l, 0)
                split(l, M_OUT + 1)
                merged_high(l, 1)

            with nc.scalar.Fori(0, L) as l:
                nc.scalar.preload_act_table_set("silu_and_others")
                split(l, 0)
                xT_high(l, 0, 0)
                square(l, 0, 0)
                square(l, 0, 1)
                ffn(l, 0)
                split(l, MIX)
                xT_high(l, 1, 0)
                square(l, 1, 0)
                square(l, 1, 1)
                mixer(l)
                split(l, FFN2)
                xT_high(l, 3, 0)
                square(l, 3, 0)
                square(l, 3, 1)
                ffn(l, 1)
            act.dma_start(bias[:], norm_final.rearrange("(o n) -> o n", o=1).broadcast_to([P, D])
                          ).then_inc(bias_landed, 16)
            square(L, 0, 0)
            square(L, 0, 1)

        @block.vector
        def _(dve):
            dve.sem_inc(lo_split, 4)
            for b in (0, 1):
                dve.sem_inc(tr_taken[b], 1)
            for i, value in enumerate((-0.5, EPS, 0.5, 1.0 / DH)):
                nc.vector.memset(small[:, i:i + 1], value).then_inc(setup_dve, 1)
            dve.wait_ge(consts_landed, 16 * 4)
            nc.vector.tensor_copy(posf[:, 0:T], pos[:, 0:T]).then_inc(setup_dve, 1)
            done = [5]

            def link(instruction):
                instruction.then_inc(setup_dve, 1)
                done[0] += 1
                dve.wait_ge(setup_dve, done[0])

            dve.wait_ge(setup_dve, done[0])
            ang, turns = sin[:, :, 0, :], sin[:, :, 1, :]
            for t in range(T):
                link(nc.vector.tensor_scalar(ang[:, t, :], inv_freq[:], posf[:, t:t + 1], None,
                                             ALU.mult))
            link(nc.vector.tensor_scalar(turns, ang, 1 / (2 * np.pi), ROUND, ALU.mult, ALU.add))
            link(nc.vector.tensor_scalar(turns, turns, ROUND, None, ALU.subtract))
            for part in TWO_PI_PARTS:
                link(nc.vector.scalar_tensor_tensor(ang, turns, -part, ang, ALU.mult, ALU.add))
            link(nc.vector.tensor_scalar(cos[:], ang, PI_BELOW, -PI_BELOW, ALU.min, ALU.max))
            assert done[0] == ANGLES_READY
            dve.wait_ge(setup_act, 2)
            link(nc.vector.tensor_tensor(cos[:], turns, turns, ALU.mult))
            link(nc.vector.tensor_scalar(cos[:], cos[:], -2.0, 1.0, ALU.mult, ALU.add))
            link(nc.vector.tensor_scalar(turns, ang, 1.0, None, ALU.mult))
            link(nc.vector.tensor_scalar(ang, ang, -1.0, None, ALU.mult))
            dve.wait_ge(x_landed, 16)
            for t in range(T):
                for b in (0, 1):
                    dve.sem_inc(taken[t][b], 1)

            def split(l, g, j=0, between=None):
                for half in (0, 1):
                    s = slice(half * HALF_AT, half * HALF_AT + vector_share(g))
                    dve.wait_ge(hi_split, l * HALVES + (j * 4 + (2 * g + half + 1)))
                    nc.vector.tensor_tensor(w_lo[:, g % 2, s], raw[:, g % 2, s],
                                            w_hi[:, g % 2, s].bitcast(F32),
                                            ALU.subtract).then_inc(lo_split, 1)
                    if half == 0 and between is not None:
                        between()

            def add_x(l, g_last, use, t, half):
                wait_product(dve, l, g_last, t)
                for n in (0, 1):
                    b = out_bank(use, n)
                    xs = x[:, t, columns(n)]
                    nc.vector.scalar_tensor_tensor(xs, acc[:, t, b, :], 0.5 if half else 1.0, xs,
                                                   ALU.mult, ALU.add).then_inc(taken[t][b], 1)

            def norm_turn(l, norm, t, between=None):
                xt_hi_at = {0: 0, 1: 4, 3: 12}[norm]
                for c in (0, 1):
                    name = ("x", norm, t, c)
                    wait_tr_full(dve, l, name)
                    if t:
                        dve.wait_ge(xT_lo_ready, l * 12 + (XT_LO_AT[norm] + c + 1))
                    col = PAR_GAIN[norm] + 4 * c
                    gain = par[:, col:col + 4].rearrange("p (k o) -> p k o", o=1)
                    nc.vector.tensor_tensor(xg[:, c, :, :],
                                            bank(name).rearrange("p (k n) -> p k n", k=4),
                                            gain.broadcast_to([P, 4, P]), ALU.mult
                                            ).then_inc(tr_taken[TR[name] % 2], 1)
                if between is not None:
                    between()
                for c in (0, 1):
                    s = (slice(None), slice(4 * c, 4 * c + 4), tokens(t))
                    dve.wait_ge(xT_hi_ready, l * 16 + (xt_hi_at + 2 * t + c + 1))
                    nc.vector.tensor_tensor(xT_lo[s], xg[:, c, :, :], xT_hi[s].bitcast(F32),
                                            ALU.subtract).then_inc(xT_lo_ready, 1)

            def merged_low(l, t):
                for c in (0, 1):
                    name = ("x", 2, t, c)
                    s = (slice(None), slice(4 * c, 4 * c + 4), tokens(t))
                    dve.wait_ge(xT_hi_ready, l * 16 + (8 + 2 * t + c + 1))
                    nc.vector.scalar_tensor_tensor(
                        xT_lo[s], bank(name).rearrange("p (k n) -> p k n", k=4), 0.5,
                        xT_hi[s].bitcast(F32), ALU.mult, ALU.subtract
                    ).then_inc(tr_taken[TR[name] % 2], 1)

            def h_low(l, f, b, j=0):
                name = ("h", f, b)
                dve.wait_ge(hT_hi_ready, l * (2 * FB) + (j * 2 + (f * FB + b + 1)))
                k = 2 * b if isinstance(j, int) else j * 4 + 2 * b
                nc.vector.tensor_tensor(hT_lo[:, bass.ds(k, 2), :],
                                        bank(name).rearrange("p (k n) -> p k n", k=2),
                                        hT_hi[:, bass.ds(k, 2), :].bitcast(F32),
                                        ALU.subtract).then_inc(tr_taken[TR[name] % 2], 1)

            def hidden(l, f, b, j=0):
                g = f * FFN2 + b
                for t in range(T):
                    dve.wait_ge(silu_ready, l * (4 * FB) + (j * 4 + (2 * FB * f + 2 * b + t + 1)))
                    nc.vector.scalar_tensor_tensor(h[:, t, :], acc[:, t, in_bank(g), 256:512],
                                                   rs[:, t:t + 1], silu_gate[:, t, :],
                                                   ALU.mult, ALU.mult
                                                   ).then_inc(taken[t][in_bank(g)], 1)

            def ffn(l, f):
                g0 = f * FFN2
                norm_turn(l, 3 * f, 1)
                split(l, g0 + 1)
                hidden(l, f, 0)
                with nc.vector.Fori(0, FB // 2) as j:
                    for b in (1, 2):
                        split(l, g0 + b + 1, j)
                        h_low(l, f, b - 1, j)
                        hidden(l, f, b, j)
                split(l, g0 + FB + 1)
                h_low(l, f, FB - 1)
                for i in range(2, len(OUT_CHUNKS)):
                    split(l, g0 + FB + i)

            def conv_taps(l, first, last):
                for i in range(first, last):
                    k, c = divmod(i, CH)
                    if i >= CH:
                        dve.wait_ge(conv_step, l * (CH * TAPS) + (i - CH + 1))
                    w = PAR_CONV_W + c * TAPS + k
                    u = uT[:, c, k:k + S]
                    if k == 0:
                        a = nc.vector.tensor_scalar(y[:, c, :], u, par[:, w:w + 1],
                                                    par[:, PAR_CONV_B + c:PAR_CONV_B + c + 1],
                                                    ALU.mult, ALU.add)
                    else:
                        a = nc.vector.scalar_tensor_tensor(y[:, c, :], u, par[:, w:w + 1],
                                                           y[:, c, :], ALU.mult, ALU.add)
                    a.then_inc(conv_step, 1)

            def gate_z(l, br, n, tiles=range(T)):
                g = M_GATE[br] + n
                b = in_bank(g)
                if n == 0:
                    dve.wait_ge(bias_landed, l * 48 + 16 * (br + 1))
                for t in tiles:
                    wait_product(dve, l, g, t)
                    nc.vector.scalar_tensor_tensor(gates[:, t, columns(n)], acc[:, t, b, :],
                                                   rs[:, t:t + 1], bias[:, columns(n)],
                                                   ALU.mult, ALU.add).then_inc(taken[t][b], 1)

            def side_low(l, name, s, k, at):
                dve.wait_ge(side_hi_ready, l * 6 + at)
                nc.vector.tensor_tensor(sideT_lo[s], bank(name).rearrange("p (k n) -> p k n", k=k),
                                        sideT_hi[s].bitcast(F32), ALU.subtract
                                        ).then_inc(tr_taken[TR[name] % 2], 1)

            def decayed(l, hd):
                name = ("scores", hd)
                dve.wait_ge(tables_landed, 32)
                wait_tr_full(dve, l, name)
                if hd >= 2:
                    dve.wait_ge(inner_done, l * HEADS + (hd - 1))
                nc.vector.tensor_tensor(st[:, hd % 2, 0:S], bank(name)[:, 0:S], decay[:, hd, :],
                                        ALU.mult)
                nc.vector.tensor_tensor(st[:, hd % 2, S:S + P], bank(name)[:, S:S + P],
                                        decay[:, hd, 0:P], ALU.mult
                                        ).then_inc(tr_taken[TR[name] % 2], 1)

            def gate_scale(l, n, t):
                dve.wait_ge(gate_ready, l * 12 + (2 * n + t + 1))
                gt = gates[:, t, columns(n)]
                nc.vector.scalar_tensor_tensor(gt, gt, 1.0, ub[:, n, :], ALU.add,
                                               ALU.mult).then_inc(gate_scaled, 1)

            def merge_first(l, t):
                wait_product(dve, l, M_POOL, t)
                for n in sorted((0, 1), key=lambda n: out_bank(M_POOL, n) != in_bank(M_GATE_RET)):
                    b = out_bank(M_POOL, n)
                    dve.wait_ge(gate_scaled, l * 4 + (2 * n + t + 1))
                    nc.vector.tensor_tensor(merged[:, t, n, :], acc[:, t, b, :],
                                            gates[:, t, columns(n)],
                                            ALU.mult).then_inc(taken[t][b], 1)

            def merge(l, br, t, done_sem):
                g = M_BRANCH[br]
                wait_product(dve, l, g, t)
                dve.wait_ge(gate_ready, l * 12 + (4 * br + 2 + t + 1))
                for n in (0, 1):
                    b = out_bank(g, n)
                    gt = gates[:, t, columns(n)]
                    nc.vector.scalar_tensor_tensor(gt, gt, 1.0, acc[:, t, b, :], ALU.add,
                                                   ALU.mult).then_inc(taken[t][b], 1)
                for n in (0, 1):
                    wait_acc_taken(dve, l, g, t, out_bank(g, n))
                    if br == RET:
                        wait_acc_taken(dve, l, M_POOL, t, out_bank(M_POOL, n))
                    else:
                        dve.wait_ge(merged_ret, l * 4 + (2 * t + n + 1))
                    m = merged[:, t, n, :]
                    nc.vector.tensor_tensor(m, m, gates[:, t, columns(n)],
                                            ALU.add).then_inc(done_sem, 1)

            def mixer(l):
                norm_turn(l, 1, 1)
                nc.vector.memset(uT[:, :, 0:PAD], 0.0).then_inc(pad_zero, 1)
                split(l, M_A + 1)
                split(l, M_B + 1)
                for t in range(T):
                    wait_acc_taken(dve, l, M_A, t, in_bank(M_A))
                    wait_acc_taken(dve, l, M_B, t, in_bank(M_B))
                    nc.vector.scalar_tensor_tensor(ua[:, t, :], ub[:, t, :], 1.0, ua[:, t, :],
                                                   ALU.add, ALU.mult).then_inc(u_ready, 1)
                split(l, M_Q + 1)
                dve.wait_ge(pad_zero, l + 1)
                for t in range(T):
                    wait_tr_taken(dve, l, ("u", t))
                taps = CH * TAPS
                conv_taps(l, 0, 12)
                split(l, M_K + 1)
                conv_taps(l, 12, 30)
                split(l, M_V + 1)
                conv_taps(l, 30, 48)
                split(l, M_G + 1)
                conv_taps(l, 48, 66)
                split(l, M_P + 1)
                conv_taps(l, 66, 82)
                split(l, M_GATE_POOL + 1)
                for i in (0, 1):
                    side_low(l, ("pooled", i), (slice(None), slice(2 * i, 2 * i + 2),
                                                slice(None)), 2, i + 1)
                gate_z(l, POOLED, 0)
                split(l, M_POOL)
                conv_taps(l, 82, 90)
                decayed(l, 0)
                decayed(l, 1)
                gate_z(l, POOLED, 1, [0])
                dve.wait_ge(scale_landed, l * 16 + 16)
                gate_scale(l, 0, 0)
                gate_scale(l, 0, 1)
                gate_scale(l, 1, 0)
                conv_taps(l, 90, 94)
                gate_z(l, POOLED, 1, [1])
                split(l, M_GATE_RET, between=lambda: merge_first(l, 0))
                decayed(l, 2)
                decayed(l, 3)
                gate_scale(l, 1, 1)
                merge_first(l, 1)
                split(l, M_GATE_RET + 1)
                conv_taps(l, 94, 112)
                dve.wait_ge(head_rs_ready, l + 1)
                for t in range(T):
                    for hd in range(HEADS):
                        s = slice(hd * P, (hd + 1) * P)
                        a = nc.vector.scalar_tensor_tensor(ua[:, t, s], ret[:, t, s],
                                                           head_rs[:, t, hd:hd + 1],
                                                           g_silu[:, t, s], ALU.mult, ALU.mult)
                    a.then_inc(ret_ready, 1)
                gate_z(l, RET, 0)
                conv_taps(l, 112, 118)
                split(l, M_RET)
                for t in range(T):
                    side_low(l, ("ret", t), (slice(None), slice(None), tokens(t)), HEADS, 3 + t)
                gate_z(l, RET, 1)
                split(l, M_GATE_CONV)
                conv_taps(l, 118, taps)
                merge(l, RET, 0, merged_ret)
                merge(l, RET, 1, merged_ret)
                split(l, M_GATE_CONV + 1)
                for t in range(T):
                    name = ("y", t)
                    wait_tr_full(dve, l, name)
                    nc.vector.bn_stats(ln_stats[:, t, :], bank(name)).then_inc(ln_stats_ready, 1)
                dve.wait_ge(ln_stats_ready, l * T + T)
                gate_z(l, CONV, 0, [0])
                for t in range(T):
                    nc.vector.bn_aggr(ln_mean_var[:, t, :], ln_stats[:, t, :]
                                      ).then_inc(ln_mean_ready, 1)
                gate_z(l, CONV, 0, [1])
                for t in range(T):
                    name = ("y", t)
                    dve.wait_ge(ln_rstd_ready, l * T + (t + 1))
                    nc.vector.tensor_scalar(pin[:, t, :], bank(name), ln_mean_var[:, t, 0:1],
                                            ln_rstd[:, t:t + 1], ALU.subtract, ALU.mult
                                            ).then_inc(tr_taken[TR[name] % 2], 1)
                split(l, M_CONV)
                for i in (0, 1):
                    s = (slice(None), slice(2 * i, 2 * i + 2), slice(None))
                    dve.wait_ge(side_hi_ready, l * 6 + (4 + i + 1))
                    nc.vector.tensor_tensor(sideT_lo[s],
                                            ysilu[:, i, :].rearrange("p (k n) -> p k n", k=2),
                                            sideT_hi[s].bitcast(F32),
                                            ALU.subtract).then_inc(conv_lo_ready, 1)
                gate_z(l, CONV, 1)
                split(l, M_OUT)
                merge(l, CONV, 0, merged_all)
                merged_low(l, 0)
                merge(l, CONV, 1, merged_all)
                split(l, M_OUT + 1)
                merged_low(l, 1)

            with nc.vector.Fori(0, L) as l:
                nc.vector.tensor_copy(par[:], all_params[:, l, :]).then_inc(par_ready, 1)
                dve.wait_ge(par_ready, l + 1)
                norm_turn(l, 0, 0, between=lambda: split(l, 0))
                ffn(l, 0)
                split(l, MIX)
                add_x(l, MIX - 1, FB, 0, True)
                norm_turn(l, 1, 0)
                add_x(l, MIX - 1, FB, 1, True)
                mixer(l)
                split(l, FFN2)
                add_x(l, FFN2 - 1, M_OUT, 0, False)
                norm_turn(l, 3, 0)
                add_x(l, FFN2 - 1, M_OUT, 1, False)
                ffn(l, 1)
                add_x(l, CHUNKS - 1, FFN2 + FB, 0, True)
                add_x(l, CHUNKS - 1, FFN2 + FB, 1, True)
            dve.wait_ge(bias_landed, 48 * L + 16)
            for t in range(T):
                dve.wait_ge(rs_ready, 6 * L + t + 1)
                for b in (0, 1):
                    dve.wait_ge(taken[t][b], L * ACC_USES[b] + 1)
                nc.vector.scalar_tensor_tensor(x[:, t, :], x[:, t, :], rs[:, t:t + 1], bias[:],
                                               ALU.mult, ALU.mult).then_inc(out_ready, 1)

        @block.gpsimd
        def _(pool):
            pool.sem_inc(lo_split_pool, 4)
            pool.wait_ge(setup_dve, 4)

            def split(l, g, j=0):
                n = half_size[g]
                for half in (0, 1):
                    s = slice(half * HALF_AT + vector_share(g), half * HALF_AT + n)
                    pool.wait_ge(hi_split, l * HALVES + (j * 4 + (2 * g + half + 1)))
                    nc.gpsimd.tensor_tensor(w_lo[:, g % 2, s], raw[:, g % 2, s],
                                            w_hi[:, g % 2, s].bitcast(F32),
                                            ALU.subtract).then_inc(lo_split_pool, 1)

            def norm_factor(l, norm):
                for t in range(T):
                    at = 2 * NORM_AT[norm] + t + 1
                    pool.wait_ge(meansq_ready, l * 6 + at)
                    nc.gpsimd.tensor_tensor(meansq_eps[:, t:t + 1], meansq[:, t:t + 1],
                                            small[:, 1:2], ALU.add).then_inc(eps_added, 1)
                    pool.wait_ge(eps_added, l * 6 + at)
                    nc.gpsimd.tensor_tensor(rs[:, t:t + 1], meansq_eps[:, t:t + 1],
                                            small[:, 0:1], ALU.pow).then_inc(pow_done, 1)
                    pool.wait_ge(pow_done, l * 6 + at)
                    nc.gpsimd.tensor_tensor(half_rs[:, t:t + 1], rs[:, t:t + 1],
                                            small[:, 2:3], ALU.mult).then_inc(rs_ready, 1)

            def ffn(l, f):
                g0 = f * FFN2
                split(l, g0 + 1)
                with nc.gpsimd.Fori(0, FB // 2) as j:
                    split(l, g0 + 2, j)
                    split(l, g0 + 3, j)
                for i in range(1, len(OUT_CHUNKS)):
                    split(l, g0 + FB + i)

            def rotary(l, i, t):
                g = M_Q + i
                a = qk[:, i, t, :].rearrange("p (h s n) -> p h s n", h=HEADS, s=2)
                r = rot[:, :, :].rearrange("p a n -> p (a n)")[:, 0:NB].rearrange(
                    "p (h s n) -> p h s n", h=HEADS, s=2)
                c = cos[:, t:t + 1, :].broadcast_to([P, 2, DH // 2])
                at = 8 * i + 4 * t
                wait_acc_taken(pool, l, g, t, in_bank(g))
                if i or t:
                    pool.wait_ge(rotary_step, l * 16 + at)
                for s in (0, 1):
                    sn = sin[:, t, s:s + 1, :].broadcast_to([P, HEADS, DH // 2])
                    nc.gpsimd.tensor_tensor(r[:, :, s, :], a[:, :, 1 - s, :], sn,
                                            ALU.mult).then_inc(rotary_step, 1)
                pool.wait_ge(rotary_step, l * 16 + (at + 2))
                for s in (0, 1):
                    cs = cos[:, t:t + 1, :].broadcast_to([P, HEADS, DH // 2])
                    op = nc.gpsimd.tensor_tensor(a[:, :, s, :], a[:, :, s, :], cs, ALU.mult)
                op.then_inc(rotary_step, 1)
                pool.wait_ge(rotary_step, l * 16 + (at + 3))
                nc.gpsimd.tensor_tensor(qk[:, i, t, :], qk[:, i, t, :],
                                        rot[:, :, :].rearrange("p a n -> p (a n)")[:, 0:NB],
                                        ALU.add).then_inc(rotary_step, 1)

            def mixer(l):
                split(l, M_A + 1)
                split(l, M_B + 1)
                split(l, M_Q + 1)
                rotary(l, 0, 0)
                rotary(l, 0, 1)
                split(l, M_K + 1)
                rotary(l, 1, 0)
                rotary(l, 1, 1)
                for g in range(M_V + 1, M_GATE_RET + 2):
                    split(l, g)
                pool.wait_ge(head_sumsq_ready, l * (T * HEADS) + T * HEADS)
                flat = [a[:].rearrange("p t h -> p (t h)")
                        for a in (head_sumsq, head_meansq, head_meansq_eps, head_rs)]
                nc.gpsimd.tensor_tensor(flat[1], flat[0], small[:, 3:4].broadcast_to([P, 8]),
                                        ALU.mult).then_inc(head_meansq_ready, 1)
                pool.wait_ge(head_meansq_ready, l + 1)
                nc.gpsimd.tensor_tensor(flat[2], flat[1], small[:, 1:2].broadcast_to([P, 8]),
                                        ALU.add).then_inc(head_eps_added, 1)
                pool.wait_ge(head_eps_added, l + 1)
                nc.gpsimd.tensor_tensor(flat[3], flat[2], small[:, 0:1].broadcast_to([P, 8]),
                                        ALU.pow).then_inc(head_rs_ready, 1)
                for g in range(M_GATE_RET + 2, M_CONV):
                    split(l, g)
                for t in range(T):
                    pool.wait_ge(ln_mean_ready, l * T + (t + 1))
                    nc.gpsimd.tensor_tensor(ln_var[:, t:t + 1], ln_mean_var[:, t, 1:2],
                                            small[:, 1:2], ALU.add).then_inc(ln_var_ready, 1)
                    pool.wait_ge(ln_var_ready, l * T + (t + 1))
                    nc.gpsimd.tensor_tensor(ln_rstd[:, t:t + 1], ln_var[:, t:t + 1],
                                            small[:, 0:1], ALU.pow
                                            ).then_inc(ln_rstd_ready, 1)
                for g in range(M_CONV, M_OUT + 2):
                    split(l, g)

            with nc.gpsimd.Fori(0, L) as l:
                split(l, 0)
                norm_factor(l, 0)
                ffn(l, 0)
                split(l, MIX)
                norm_factor(l, 1)
                mixer(l)
                split(l, FFN2)
                norm_factor(l, 3)
                ffn(l, 1)
            norm_factor(L, 0)


def decay_table():
    log_gamma = np.log1p(-(2.0 ** (-5.0 - np.arange(HEADS))))
    diff = np.arange(S)[None, :] - np.arange(P)[:, None]
    d = np.exp(log_gamma[None, :, None] * np.maximum(diff, 0)[:, None, :])
    return np.where(diff[:, None, :] >= 0, d * DH ** -0.5, 0.0).astype(np.float32)


def band_table():
    m = np.zeros((S, GROUPS, S))
    for g, w in enumerate(WINDOWS):
        for t in range(S):
            n = min(t + 1, w)
            m[t - n + 1:t + 1, g, t] = 1.0 / n
            m[t, g, t] -= 1.0
    return np.concatenate([m[:P], m[P:, :, P:]], axis=2).astype(np.float32)


def inv_freq_table():
    half = DH // 2
    f = np.float32(ROPE_BASE) ** (-np.arange(half, dtype=np.float32) / np.float32(half))
    return np.ascontiguousarray(np.broadcast_to(f.astype(np.float32), (P, half)))


def in_order_of_use(w):
    stream = np.zeros((L, HALVES, P, 2048), np.float32)

    def put(g, tiles):
        m = tiles.shape[1] // 2
        for half in (0, 1):
            part = tiles[:, half * m:(half + 1) * m].transpose(0, 2, 1, 3).reshape(L, P, -1)
            stream[:, 2 * g + half, :, :part.shape[2]] = part

    for g0, n in ((0, "1"), (FFN2, "2")):
        w_i = w[f"w_ffn{n}_in"].reshape(L, KT, P, 2, FB, 256)
        w_o = w[f"w_ffn{n}_out"].reshape(L, FT, P, D)
        for b in range(FB):
            put(g0 + b, w_i[:, :, :, :, b].reshape(L, KT, P, NB))
        for i, ks in enumerate(OUT_CHUNKS):
            put(g0 + FB + i, w_o[:, ks[0]:ks[-1] + 1])
    for g, c in W_IN_BLOCK.items():
        put(g, w["w_in"].reshape(L, KT, P, -1, NB)[:, :, :, c])
    put(M_POOL, w["w_pool"])
    put(M_RET, w["w_ret_out"].reshape(L, 4, P, D))
    put(M_CONV, w["w_conv_out"].reshape(L, 4, P, D))
    for i in (0, 1):
        put(M_OUT + i, w["w_out"].reshape(L, KT, P, D)[:, 4 * i:4 * i + 4])
    return stream.reshape(-1)


def kernel(**inputs):
    import concourse.bacc as bacc
    from concourse.bass_utils import run_bass_kernel_spmd

    arrays = {"x": np.asarray(inputs["x"]),
              "positions": np.ascontiguousarray(np.asarray(inputs["positions"]).reshape(T, P).T),
              "weights": in_order_of_use({n: np.asarray(a) for n, a in inputs.items()})}
    for name in ("gate_bias", "pool_scale", "norm_final"):
        arrays[name] = np.asarray(inputs[name])

    def by_feature(name):
        a = np.asarray(inputs[name])
        return a.reshape(L, -1, P).transpose(0, 2, 1)

    conv_w = np.asarray(inputs["conv_w"]).reshape(L, TAPS, CH, P).transpose(0, 3, 2, 1)
    arrays["params"] = np.concatenate(
        [by_feature("norm_ffn1"), by_feature("norm_mix"), by_feature("norm_ffn2"),
         conv_w.reshape(L, P, CH * TAPS), by_feature("conv_b"), by_feature("conv_ln_g"),
         by_feature("conv_ln_b")], axis=2)
    arrays["ident"] = np.eye(P, dtype=np.float32)
    arrays["inv_freq"] = inv_freq_table()
    arrays["decay"] = decay_table()
    arrays["band"] = band_table()

    nc = bacc.Bacc("TRN2", target_bir_lowering=False, num_devices=1)
    aps = [nc.dram_tensor(f"in_{name}", a.shape, mybir.dt.from_np(a.dtype),
                          kind="ExternalInput").ap() for name, a in arrays.items()]
    out = nc.dram_tensor("out", [1, S, D], F32, kind="ExternalOutput").ap()
    trunk(nc, *aps, out)
    r = run_bass_kernel_spmd(nc, [{f"in_{name}": a for name, a in arrays.items()}], core_ids=[0])
    return r.results[0]["out"]
```
